# Optimizing a Trainium2 kernel written in Bass

```python
import math
import jax, jax.numpy as jnp
from jax import lax
import numpy as np

D_MODEL = 1024
BATCH = 1
SEQ = 512
DEPTH = 1
DEC_BATCH = 1
DEC_SEQ = 512
PAST_LEN = 128

HEAD_DIM = 64
MIX_WIDTH = D_MODEL
A_WIDTH = MIX_WIDTH // 2
B_WIDTH = MIX_WIDTH - A_WIDTH
A_HEADS = A_WIDTH // HEAD_DIM
A_KV_HEADS = A_HEADS // 4
A_GROUP = A_HEADS // A_KV_HEADS
B_HEADS = B_WIDTH // HEAD_DIM
Q_BLOCK = 128
GRID_W = 64
WIN_ROWS = 8
WIN_COLS = 16
ROPE_THETA = 10000.0
ROPE_AXIS_DIM = HEAD_DIM // 2
D_FF = 4 * D_MODEL
EPS = 1e-6
IN_COLS = A_WIDTH + 2 * A_KV_HEADS * HEAD_DIM + 3 * B_WIDTH

kernel_name = "hybrid_gqa_axialrope_natten_encoder"

def rms_norm(x, g):
    xf = x.astype(jnp.float32)
    y = xf * lax.rsqrt(jnp.mean(xf * xf, axis=-1, keepdims=True) + EPS)
    return (y * g.astype(jnp.float32)).astype(x.dtype)

def rope_1d(x, pos):
    half = x.shape[-1] // 2
    freqs = ROPE_THETA ** (-jnp.arange(half, dtype=jnp.float32) / half)
    ang = pos.astype(jnp.float32)[:, None] * freqs[None, :]
    cos = jnp.cos(ang).astype(x.dtype)
    sin = jnp.sin(ang).astype(x.dtype)
    x1, x2 = x[..., :half], x[..., half:]
    return jnp.concatenate([x1 * cos - x2 * sin, x1 * sin + x2 * cos], axis=-1)

def rope_2d_axial(x, seq_len):
    t = jnp.arange(seq_len, dtype=jnp.int32)
    row, col = t // GRID_W, t % GRID_W
    return jnp.concatenate([rope_1d(x[..., :ROPE_AXIS_DIM], row),
                            rope_1d(x[..., ROPE_AXIS_DIM:], col)], axis=-1)

def global_gqa_attention(q, k, v):
    b, kvh, g, s, dh = q.shape
    nb = s // Q_BLOCK
    scale = dh ** -0.5
    qb = q.reshape(b, kvh, g, nb, Q_BLOCK, dh).transpose(3, 0, 1, 2, 4, 5)

    def one_block(q_blk):
        sc = jnp.einsum('bkgqd,bksd->bkgqs', q_blk, k).astype(jnp.float32) * scale
        p = jax.nn.softmax(sc, axis=-1).astype(v.dtype)
        return jnp.einsum('bkgqs,bksd->bkgqd', p, v)

    o = lax.map(one_block, qb)
    o = o.transpose(1, 0, 4, 2, 3, 5)
    return o.reshape(b, s, kvh * g * dh)

def neighbourhood_tables(rows):
    wr = min(WIN_ROWS, rows)
    s = rows * GRID_W
    t = np.arange(s)
    r, c = t // GRID_W, t % GRID_W
    rs = np.clip(r - wr // 2, 0, rows - wr)
    cs = np.clip(c - WIN_COLS // 2, 0, GRID_W - WIN_COLS)
    kr = rs[:, None, None] + np.arange(wr)[None, :, None]
    kc = cs[:, None, None] + np.arange(WIN_COLS)[None, None, :]
    kr, kc = np.broadcast_arrays(kr, kc)
    n_keys = wr * WIN_COLS
    idx = (kr * GRID_W + kc).reshape(s, n_keys)
    dr = (kr - r[:, None, None] + (WIN_ROWS - 1)).reshape(s, n_keys)
    dc = (kc - c[:, None, None] + (WIN_COLS - 1)).reshape(s, n_keys)
    return (jnp.asarray(idx, jnp.int32), jnp.asarray(dr, jnp.int32),
            jnp.asarray(dc, jnp.int32), n_keys)

def neighbourhood_attention(q, k, v, rel_bias, rows):
    b, hb, s, dh = q.shape
    idx, dr, dc, n_keys = neighbourhood_tables(rows)
    scale = dh ** -0.5
    bias = rel_bias.astype(jnp.float32)[:, dr, dc]
    bias = bias.reshape(hb, rows, GRID_W, n_keys).transpose(1, 0, 2, 3)
    qr = q.reshape(b, hb, rows, GRID_W, dh).transpose(2, 0, 1, 3, 4)
    idx_r = idx.reshape(rows, GRID_W, n_keys)

    def one_row(args):
        q_blk, idx_blk, bias_blk = args
        kg = jnp.take(k, idx_blk, axis=2)
        vg = jnp.take(v, idx_blk, axis=2)
        sc = jnp.einsum('bhqd,bhqkd->bhqk', q_blk, kg).astype(jnp.float32) * scale
        p = jax.nn.softmax(sc + bias_blk[None], axis=-1).astype(v.dtype)
        return jnp.einsum('bhqk,bhqkd->bhqd', p, vg)

    o = lax.map(one_row, (qr, idx_r, bias))
    o = o.transpose(1, 0, 3, 2, 4)
    return o.reshape(b, s, hb * dh)

def hybrid_layer(x, norm_attn_g, w_in, q_norm_g, k_norm_g, nat_rel_bias,
                 out_norm_a_g, out_norm_b_g, w_out, norm_mlp_g, w_up, w_down):
    b, s, _ = x.shape
    rows = s // GRID_W
    h = rms_norm(x, norm_attn_g)
    proj = h @ w_in
    kv_w = A_KV_HEADS * HEAD_DIM
    o1 = A_WIDTH
    o2 = o1 + kv_w
    o3 = o2 + kv_w
    o4 = o3 + B_WIDTH
    o5 = o4 + B_WIDTH
    qa = proj[..., :o1].reshape(b, s, A_KV_HEADS, A_GROUP, HEAD_DIM).transpose(0, 2, 3, 1, 4)
    ka = proj[..., o1:o2].reshape(b, s, A_KV_HEADS, HEAD_DIM).transpose(0, 2, 1, 3)
    va = proj[..., o2:o3].reshape(b, s, A_KV_HEADS, HEAD_DIM).transpose(0, 2, 1, 3)
    qa = rope_2d_axial(rms_norm(qa, q_norm_g), s)
    ka = rope_2d_axial(rms_norm(ka, k_norm_g), s)
    ya = global_gqa_attention(qa, ka, va)
    qb = proj[..., o3:o4].reshape(b, s, B_HEADS, HEAD_DIM).transpose(0, 2, 1, 3)
    kb = proj[..., o4:o5].reshape(b, s, B_HEADS, HEAD_DIM).transpose(0, 2, 1, 3)
    vb = proj[..., o5:].reshape(b, s, B_HEADS, HEAD_DIM).transpose(0, 2, 1, 3)
    yb = neighbourhood_attention(qb, kb, vb, nat_rel_bias, rows)
    y = jnp.concatenate([rms_norm(ya, out_norm_a_g), rms_norm(yb, out_norm_b_g)], axis=-1)
    x = x + y @ w_out
    u = rms_norm(x, norm_mlp_g) @ w_up
    u = jnp.square(jax.nn.relu(u))
    return x + u @ w_down

def setup_inputs(seed: int = 0) -> dict:
    key = jax.random.key(seed)
    ks = jax.random.split(key, 16)
    f32 = jnp.float32

    def gain(k, shape):
        return (1.0 + 0.02 * jax.random.normal(k, shape)).astype(f32)

    def weight(k, shape, fan_in):
        return (jax.random.normal(k, shape) * fan_in ** -0.5).astype(f32)

    return {
        "x_prompt": jax.random.normal(ks[0], (BATCH, SEQ, D_MODEL), f32),
        "x_sample": jax.random.normal(ks[1], (DEC_BATCH, DEC_SEQ, D_MODEL), f32),
        "norm_attn_g": gain(ks[2], (DEPTH, D_MODEL)),
        "w_in": weight(ks[3], (DEPTH, D_MODEL, IN_COLS), D_MODEL),
        "q_norm_g": gain(ks[4], (DEPTH, HEAD_DIM)),
        "k_norm_g": gain(ks[5], (DEPTH, HEAD_DIM)),
        "nat_rel_bias": (0.1 * jax.random.normal(ks[6], (DEPTH, B_HEADS, 2 * WIN_ROWS - 1, 2 * WIN_COLS - 1))).astype(f32),
        "out_norm_a_g": gain(ks[7], (DEPTH, A_WIDTH)),
        "out_norm_b_g": gain(ks[8], (DEPTH, B_WIDTH)),
        "w_out": weight(ks[9], (DEPTH, MIX_WIDTH, D_MODEL), MIX_WIDTH),
        "norm_mlp_g": gain(ks[10], (DEPTH, D_MODEL)),
        "w_up": weight(ks[11], (DEPTH, D_MODEL, D_FF), D_MODEL),
        "w_down": weight(ks[12], (DEPTH, D_FF, D_MODEL), D_FF),
        "final_norm_g": gain(ks[13], (D_MODEL,)),
    }

def encoder(x, norm_attn_g, w_in, q_norm_g, k_norm_g, nat_rel_bias, out_norm_a_g,
            out_norm_b_g, w_out, norm_mlp_g, w_up, w_down, final_norm_g):
    for l in range(DEPTH):
        x = hybrid_layer(x, norm_attn_g[l], w_in[l], q_norm_g[l], k_norm_g[l],
                         nat_rel_bias[l], out_norm_a_g[l], out_norm_b_g[l], w_out[l],
                         norm_mlp_g[l], w_up[l], w_down[l])
    return rms_norm(x, final_norm_g)

def reference(x_prompt, x_sample, norm_attn_g, w_in, q_norm_g, k_norm_g, nat_rel_bias,
              out_norm_a_g, out_norm_b_g, w_out, norm_mlp_g, w_up, w_down, final_norm_g):
    y_prompt = encoder(x_prompt, norm_attn_g, w_in, q_norm_g, k_norm_g, nat_rel_bias,
                       out_norm_a_g, out_norm_b_g, w_out, norm_mlp_g, w_up, w_down,
                       final_norm_g)
    y_sample = encoder(x_sample, norm_attn_g, w_in, q_norm_g, k_norm_g, nat_rel_bias,
                       out_norm_a_g, out_norm_b_g, w_out, norm_mlp_g, w_up, w_down,
                       final_norm_g)
    return (y_prompt, y_sample)


_drawn_inputs = setup_inputs


def setup_inputs(seed=0):
    import zlib

    import numpy as np

    out = dict(_drawn_inputs(seed))
    spreads = {}
    factors = {'q_norm_g': 5.538,
     'k_norm_g': 4.674,
     'out_norm_a_g': 5.317,
     'out_norm_b_g': 5.513,
     'norm_mlp_g': 3.856,
     'final_norm_g': 2.729}
    for name, (base, spread) in spreads.items():
        noise = np.random.default_rng([zlib.crc32(name.encode()), seed]).standard_normal(out[name].shape)
        drawn = base * np.exp(spread * noise) if base else spread * noise
        out[name] = __import__('jax').numpy.asarray(drawn.astype(out[name].dtype))
    for name, factor in factors.items():
        out[name] = (out[name] * factor).astype(out[name].dtype)
    return out
```

```python
from contextlib import ExitStack

import numpy as np

import concourse.bass as bass
from concourse import mybir

F32 = mybir.dt.float32
F32R = mybir.dt.float32r
ALU = mybir.AluOpType
ACT = mybir.ActivationFunctionType
AX_X = mybir.AxisListType.X

P = 128
D = 1024
SEQ = 512
NB = 2
TOK = NB * SEQ
NT = TOK // P
TPB = NT // NB
DT = D // P
HD = 64
AH, KVH, BH = 8, 2, 8
GW, GH = 64, 8
WC = 16
COLS_PER_TILE = P // GH
FF = 4 * D
EPS = 1e-6
QSCALE = HD ** -0.5
MASKED = -1e30

QA0, KA0, VA0 = 0, AH * HD, AH * HD + KVH * HD
QB0 = VA0 + KVH * HD
KB0, VB0 = QB0 + BH * HD, QB0 + 2 * BH * HD
TQA, TKA, TVA, TVB = 0, 512, 640, 768
TMW = 1280
BROW, BLEN, BPAD = 2 * WC - 1, 480, 7
NZ = 2 * WC - 1
KW = 256
B_KEY_COL = [0, 8, 24, 32]
B_VARIANT = [0, 1, 1, 2]
B_VALID = [(0, 8, 23), (0, 0, 31), (8, 0, 24)]

PC = 512
RAW_SLOTS = 4
W_SLOTS = 4
FC = 512
NCHUNK = FF // FC
FT = FC // P

QKW = (AH + KVH) * HD
NSTEP = NB * (AH + BH) * TPB
LAG_T, LAG_V = 3, 4
LAG_BACK = LAG_V + 3
S_BANKS, PT_BANKS, O_BANKS, BACK_BANK = (0, 1, 2), (3, 4), (5, 6), 7
PROB_SLOTS, PT_SLOTS = 4, 3


class Block:

    def __init__(self, what, weight, col0, width, seqs, banks, weave=None):
        self.what, self.weight, self.col0, self.width = what, weight, col0, width
        self.seqs, self.banks = seqs, banks
        self.weave = weave


FM_BANKS = [4 * b + j for j in range(4) for b in range(NB)]
OUT_BANKS = 6
BLOCKS = [
    Block("qa", "w_in", QA0, 512, (0,), [0, 1, 2, 3], (0, 1)),
    Block("qa", "w_in", QA0, 512, (1,), [4, 5, 6, 7]),
    Block("kv", "w_in", KA0, 256, (0, 1), list(range(8))),
    Block("vb", "w_in", VB0, 512, (0, 1), list(range(8))),
    Block("qb", "w_in", QB0, 512, (0, 1), FM_BANKS),
    Block("kb", "w_in", KB0, 512, (0, 1), FM_BANKS),
] + [
    Block("out", "w_out", half * PC, PC, (b,), [(4 * (2 * b + half) + j) % OUT_BANKS for j in range(4)],
          {(0, 0): (1, 1), (1, 0): (2, 0)}.get((b, half)))
    for b in range(NB) for half in range(2)
] + [
    Block("up", "w_up", 0, PC, (0,), [0, 1, 2, 3], (2, 1)),
    Block("up", "w_up", 0, PC, (1,), [4, 5, 6, 7]),
]
N_PJ, N_OUT = 6, 4
PIECE_OUT = N_PJ * DT
PIECE_UP = PIECE_OUT + N_OUT * DT
PIECE_DOWN = PIECE_UP + NB * DT
PIECE_LOOP = PIECE_DOWN + 2 * FT
PER_CHUNK = DT + 2 * FT
FULL_BEFORE = [sum(len(x.banks) - 1 for x in BLOCKS[:i]) for i in range(len(BLOCKS) + 1)]
FULL_DOWN = FULL_BEFORE[-1]
FULL_LOOP = FULL_DOWN + 2 * (NT - 1)
FULL_CHUNK = 3 * (NT - 1)
NORM_BANKS = {(0, 0): [4, 5, 6, 7], (0, 1): [4, 5, 6, 7], (1, 0): [0, 1, 2, 3], (1, 1): [6, 7],
              (2, 0): [6, 7], (2, 1): [6, 7]}
HSUM_AT = 3 * DT + 4 + 1


def shape_constants():
    t = np.arange(SEQ)
    col, row = t // GH, t % GH
    half = HD // 4
    freqs = (10000.0 ** (-np.arange(half, dtype=np.float32) / np.float32(half))).astype(np.float32)
    cos = np.zeros((SEQ, 2, 2, half), np.float32)
    sin = np.zeros((SEQ, 2, 2, half), np.float32)
    for axis, pos in enumerate((row, col)):
        ang = (pos.astype(np.float32)[:, None] * freqs[None, :]).astype(np.float32)
        cos[:, axis, 0] = cos[:, axis, 1] = np.cos(ang.astype(np.float64))
        sin[:, axis, 0] = -np.sin(ang.astype(np.float64))
        sin[:, axis, 1] = np.sin(ang.astype(np.float64))
    rope = np.stack([cos.reshape(TPB, P, HD), sin.reshape(TPB, P, HD)], 0)
    rope = np.ascontiguousarray(rope.transpose(2, 0, 1, 3)).reshape(P, 2 * TPB * HD)
    mask = np.full((P, 3, NZ, GH), MASKED, np.float32)
    b = np.arange(P) // GH
    for v, tile in enumerate((0, 1, TPB - 1)):
        qc = tile * COLS_PER_TILE + b
        cs = np.clip(qc - WC // 2, 0, GW - WC)
        for z in range(NZ):
            kc = tile * COLS_PER_TILE - WC // 2 + z
            mask[(kc >= cs) & (kc < cs + WC), v, z, :] = 0.0
    return rope, mask.reshape(P, 3 * NZ * GH), np.eye(P, dtype=np.float32)


def encoder_program(nc, xs_in, w_in, bias_tab, gains, qk_gains, w_out, w_up, w_down,
                    rope_c, mask_c, ident_c, ys_out):
    with ExitStack() as ctx:
        def sb(name, shape, dt=F32, where=ctx):
            return where.enter_context(nc.sbuf_tensor(name, shape, dt))

        def sem(name):
            return ctx.enter_context(nc.semaphore(name))

        ident = sb("ident", [P, P])
        gain = sb("gain", [P, D])
        stat = sb("stat", [P, 4, NT, 2])
        half_ms = sb("half_ms", [P, NT])
        rms = sb("rms", [P, 4, NT, 2])
        rstd = sb("rstd", [P, 4, NT, 2])
        eps = sb("eps", [P, 1])
        w_raw = sb("w_raw", [P, RAW_SLOTS, PC])
        w_hi = sb("w_hi", [P, W_SLOTS, PC], F32R)
        w_lo = sb("w_lo", [P, W_SLOTS, PC], F32R)
        biasm = sb("biasm", [P, 3, BH, KW])
        rope = sb("rope", [P, 2, TPB, HD])
        qkg = sb("qkg", [P, 4, HD])
        tab = sb("tab", [P, 4, TPB, HD])
        hss = sb("hss", [P, NT, AH + KVH])

        space = ExitStack()
        rt = sb("rt", [P, 3, QKW], F32, space)
        space.close()
        xn = sb("xn", [P, 2, D])

        space = ExitStack()
        u_hi = sb("u_hi", [P, FT, TOK], F32R, space)
        u_lo = sb("u_lo", [P, FT, TOK], F32R, space)
        relu = sb("relu", [P, 2, PC], F32, space)
        sq = sb("sq", [P, 2, PC], F32, space)
        space.close()
        pj = sb("pj", [P, NT, TMW])

        space = ExitStack()
        mask = sb("mask", [P, 3, NZ * GH], F32, space)
        bias_raw = sb("bias_raw", [P, BH, GH * NZ], F32, space)
        space.close()
        space = ExitStack()
        qkb = sb("qkb", [P, 2 * BH * HD // P, TOK], F32, space)
        space.close()
        xr = sb("xr", [P, NT, D])

        space = ExitStack()
        q_hl = sb("q_hl", [P, AH, SEQ], F32R, space)
        k_hh = sb("k_hh", [P, KVH, SEQ], F32R, space)
        k_lo = sb("k_lo", [P, SEQ], F32R, space)
        vsh = sb("vsh", [P, NB, 3, BH * HD], F32, space)
        sB = sb("sB", [P, PROB_SLOTS, KW], F32, space)
        prob = sb("prob", [P, PROB_SLOTS, SEQ], F32, space)
        probT = sb("probT", [P, PT_SLOTS, SEQ], F32, space)
        oT = sb("oT", [HD, 2, SEQ], F32, space)
        negmax = sb("negmax", [P, NSTEP], F32, space)
        psums = sb("psums", [P, NSTEP], F32, space)
        pinv = sb("pinv", [P, NSTEP], F32, space)
        space.close()
        space = ExitStack()
        yo = sb("yo", [P, NT, D], F32, space)
        junk = sb("junk", [P, NT, D], F32, space)
        space.close()
        hT_hi = sb("hT_hi", [P, DT, TOK], F32R)
        hT_lo = sb("hT_lo", [P, DT, TOK], F32R)

        ps = [ctx.enter_context(nc.psum_tensor(f"ps{i}", [P, PC], F32)) for i in range(8)]

        xg_ready = sem("xg_ready")
        half_ready = sem("half_ready")
        qk_lo_ready = sem("qk_lo_ready")
        x_landed = [sem(f"x_landed{t}") for t in range(NT)]
        w_landed = [sem(f"w_landed{s}") for s in range(RAW_SLOTS)]
        const_landed = sem("const_landed")
        pool_landed = sem("pool_landed")
        gain_landed = sem("gain_landed")
        vsh_landed = sem("vsh_landed")
        xr_landed = sem("xr_landed")
        y_stored = sem("y_stored")
        hi_split = sem("hi_split")
        lo_split = sem("lo_split")
        w_used = sem("w_used")
        bank_full = sem("bank_full")
        act_evac = sem("act_evac")
        dve_evac = sem("dve_evac")
        sumsq = sem("sumsq")
        rms_ready = sem("rms_ready")
        rstd_ready = sem("rstd_ready")
        eps_ready = sem("eps_ready")
        hrms_ready = sem("hrms_ready")
        xn_ready = sem("xn_ready")
        xT_ready = sem("xT_ready")
        hT_hi_ready = sem("hT_hi_ready")
        hT_lo_ready = sem("hT_lo_ready")
        pool_step = sem("pool_step")
        bias_ready = sem("bias_ready")
        hstat = sem("hstat")
        hstat_ready = sem("hstat_ready")
        rope_done = sem("rope_done")
        s_ready = sem("s_ready")
        biased = sem("biased")
        max_ready = sem("max_ready")
        p_ready = sem("p_ready")
        pt_ready = sem("pt_ready")
        pt_copied = sem("pt_copied")
        pv_done = sem("pv_done")
        oT_ready = sem("oT_ready")
        back_ready = sem("back_ready")
        inv_ready = sem("inv_ready")
        y_written = sem("y_written")
        sq_ready = sem("sq_ready")
        u_hi_ready = sem("u_hi_ready")
        u_lo_ready = sem("u_lo_ready")
        xo_ready = sem("xo_ready")

        block = ctx.enter_context(nc.Block())

        def over(ap, axis, n):
            shape = list(ap.shape)
            return ap.unsqueeze(axis).to_broadcast(shape[:axis] + [n] + shape[axis:])

        def tok_rows(dram, t):
            rows = dram.rearrange("(r c) d -> c r d", r=GH)
            c0 = (t % TPB) * COLS_PER_TILE
            return rows[c0:c0 + COLS_PER_TILE, :, :]

        def w_piece(n):
            if n < PIECE_DOWN:
                blk, d = BLOCKS[n // DT], n % DT
                dram = {"w_in": w_in, "w_out": w_out, "w_up": w_up}[blk.weight]
                return dram[d * P:(d + 1) * P, blk.col0:blk.col0 + blk.width], blk.width
            half, k = (n - PIECE_DOWN) // FT, (n - PIECE_DOWN) % FT
            return w_down[k * P:(k + 1) * P, half * PC:(half + 1) * PC], PC

        def split_waits_raw(eng, n, slot):
            eng.wait_ge(w_landed[slot], (n - slot) * (16 // RAW_SLOTS) + 16)

        def wait_bank(eng, full_before, pos, nbanks, last_piece):
            if pos < nbanks - 1:
                eng.wait_ge(bank_full, full_before + (pos + 1))
            else:
                eng.wait_ge(w_used, last_piece + 1)

        ACT0, DVE0 = 20, 20
        DVE1 = DVE0 + 2 * NT
        UP_ACT, UP_DVE, DN_DVE = 4, 4, 2 * NT
        CH_DVE = UP_DVE + DN_DVE

        @block.sync
        def _(sp):
            def load_x(t, dst, landed):
                sp.dma_start(dst, tok_rows(xs_in[t // TPB], t)).then_inc(landed, 16)

            def load_piece(n, src, width, slot):
                if not isinstance(n, int) or n >= RAW_SLOTS:
                    sp.wait_ge(lo_split, n - RAW_SLOTS + 1)
                sp.dma_start(w_raw[:, slot, 0:width], src).then_inc(w_landed[slot], 16)

            def load_pieces(n0, n1):
                for n in range(n0, n1):
                    src, width = w_piece(n)
                    load_piece(n, src, width, n % RAW_SLOTS)

            def load_gain(m):
                if m:
                    sp.wait_ge(xn_ready, m * NT)
                sp.dma_start(gain[:, :], gains[m:m + 1, :].to_broadcast([P, D])).then_inc(gain_landed, 16)

            load_x(0, pj[:, 0, 0:D], x_landed[0])
            load_gain(0)
            sp.dma_start(ident[:, :], ident_c).then_inc(const_landed, 16)
            for t in range(1, TPB):
                load_x(t, pj[:, t, 0:D], x_landed[t])
                load_pieces(t - 1, t)
            load_pieces(TPB - 1, RAW_SLOTS)
            for t in range(TPB, NT):
                load_x(t, pj[:, t, 0:D], x_landed[t])
            load_pieces(RAW_SLOTS, NT)
            sp.dma_start(rope[:, :, :, :].rearrange("p a t d -> p (a t d)"), rope_c).then_inc(pool_landed, 16)
            sp.dma_start(qkg[:, :, :].rearrange("p a d -> p (a d)"),
                         qk_gains[0:1, :].to_broadcast([P, 4 * HD])).then_inc(pool_landed, 16)
            sp.dma_start(mask[:, :, :].rearrange("p v z -> p (v z)"), mask_c).then_inc(pool_landed, 16)
            for h in range(BH):
                src = bass.AP(bias_tab.tensor, h * BLEN, [[1, COLS_PER_TILE], [BROW, GH], [1, GH * NZ]])
                sp.dma_start(bias_raw[:, h, :], src).then_inc(pool_landed, 16)
                load_pieces(NT + h, NT + h + 1)
            load_pieces(2 * NT, 3 * NT)
            load_gain(1)
            load_pieces(3 * NT, PIECE_OUT + 2 * RAW_SLOTS - 1)
            sp.wait_ge(w_used, PIECE_OUT)
            sp.wait_ge(act_evac, ACT0)
            sp.wait_ge(dve_evac, DVE0)
            for b in range(NB):
                t0 = b * TPB
                sp.dma_start(vsh[0:64, b, :, :], pj[64:P, t0:t0 + 3, TVB:TMW]).then_inc(vsh_landed, 16)
                sp.dma_start(vsh[64:P, b, :, :], pj[0:64, t0 + 1:t0 + 4, TVB:TMW]).then_inc(vsh_landed, 16)
            sp.wait_ge(s_ready, NSTEP)
            for t in range(NT):
                load_x(t, xr[:, t, :], xr_landed)
            load_pieces(PIECE_OUT + 2 * RAW_SLOTS - 1, PIECE_OUT + 2 * DT - 4)
            load_gain(2)
            load_pieces(PIECE_OUT + 2 * DT - 4, PIECE_LOOP)
            load_gain(3)
            with sp.Fori(1, NCHUNK) as c:
                base = c * PER_CHUNK + (PIECE_LOOP - PER_CHUNK)
                for k in range(DT):
                    load_piece(base + k, w_up[k * P:(k + 1) * P, bass.ds(c * FC, FC)], PC, k % RAW_SLOTS)
                for half in range(2):
                    for k in range(FT):
                        n = DT + half * FT + k
                        load_piece(base + n, w_down[bass.ds(c * FC + k * P, P), half * PC:(half + 1) * PC],
                                   PC, n % RAW_SLOTS)
            for t in range(NT):
                sp.wait_ge(xo_ready, t + 1)
                sp.dma_start(tok_rows(ys_out[t // TPB], t), yo[:, t, :]).then_inc(y_stored, 16)
            sp.wait_ge(y_stored, 16 * NT)

        def norm_src(m, t):
            if m == 0:
                return [(pj[:, t, 0:D], 0, D)]
            if m == 1:
                return [(pj[:, t, 0:D // 2], 0, D // 2), (pj[:, t, TVB:TMW], D // 2, D)]
            return [(xr[:, t, :], 0, D)]

        SQ0 = [0, NT, 3 * NT, 4 * NT]

        def norm_src_wait(eng, m, t):
            if m == 0:
                eng.wait_ge(x_landed[t], 16)
            elif m == 1:
                eng.wait_ge(y_written, (t // TPB + 1) * (AH + BH))
            else:
                eng.wait_ge(dve_evac, DVE0 + NT * (t // TPB) + TPB + t % TPB + 1)

        def act_square(act, m, t):
            norm_src_wait(act, m, t)
            if m * NT + t >= 2:
                act.wait_ge(xT_ready, 2 * (m * NT + t - 1))
            parts = norm_src(m, t)
            for g, (src, c0, c1) in enumerate(parts):
                nc.scalar.activation(xn[:, t % 2, c0:c1], src, ACT.Square,
                                     accum_out=stat[:, m, t, g:g + 1]).then_inc(sumsq, 1)
            n = len(parts)
            act.wait_ge(sumsq, SQ0[m] + (t + 1) * n)
            nc.scalar.activation(rms[:, m, t, 0:n], stat[:, m, t, 0:n], ACT.Sqrt, bias=eps[:, 0:1],
                                 scale=1.0 / (c1 - c0)).then_inc(rms_ready, 1)

        def norm_bank(m, t, j):
            banks = NORM_BANKS[m, t // TPB]
            return ps[banks[(2 * (t % TPB) + j) % len(banks)]]

        def hT_part(hT, t, j):
            return hT[:, 4 * j:4 * j + 4, t * P:(t + 1) * P]

        def act_hT_hi(act, m, t):
            for j in range(2):
                act.wait_ge(xT_ready, 2 * (m * NT + t) + j + 1)
                nc.scalar.copy(hT_part(hT_hi, t, j),
                               norm_bank(m, t, j)[:, :].rearrange("p (d q) -> p d q", q=P)).then_inc(hT_hi_ready, 1)

        def dve_norm(dve, m, t):
            parts = norm_src(m, t)
            e = m * NT + t
            n = len(parts)
            dve.wait_ge(rms_ready, e + 1)
            nc.vector.reciprocal(rstd[:, m, t, 0:n], rms[:, m, t, 0:n]).then_inc(rstd_ready, 1)
            dve.wait_ge(rstd_ready, e + 1)
            if t == 0:
                dve.wait_ge(gain_landed, 16 * (m + 1))
            for g, (src, c0, c1) in enumerate(parts):
                last = nc.vector.scalar_tensor_tensor(xn[:, t % 2, c0:c1], src, rstd[:, m, t, g:g + 1],
                                                      gain[:, c0:c1], ALU.mult, ALU.mult)
            last.then_inc(xn_ready, 1)

        def dve_hT_lo(dve, m, t):
            for j in range(2):
                dve.wait_ge(hT_hi_ready, 2 * (m * NT + t) + j + 1)
                nc.vector.tensor_tensor(hT_part(hT_lo, t, j),
                                        norm_bank(m, t, j)[:, :].rearrange("p (d q) -> p d q", q=P),
                                        hT_part(hT_hi, t, j).bitcast(F32), ALU.subtract).then_inc(hT_lo_ready, 1)

        def pe_norm(pe, m, t):
            e = m * NT + t
            nbanks = len(NORM_BANKS[m, t // TPB])
            pe.wait_ge(xn_ready, e + 1)
            if 2 * (t % TPB) >= nbanks:
                pe.wait_ge(hT_lo_ready, 2 * e - nbanks + 2)
            elif e % TPB == 0 and e:
                pe.wait_ge(hT_lo_ready, 2 * e)
            for j in range(2):
                for d in range(4):
                    last = nc.tensor.transpose(norm_bank(m, t, j)[:, d * P:(d + 1) * P],
                                               xn[:, t % 2, (4 * j + d) * P:(4 * j + d + 1) * P], ident[:, :])
                last.then_inc(xT_ready, 1)

        def norm_alone(m, b, mine, lag, also=None):
            for t in range(b * TPB, (b + 1) * TPB + 1):
                if t < (b + 1) * TPB:
                    mine(m, t)
                if t > b * TPB:
                    lag(m, t - 1)
                    if also:
                        also(t - 1)

        def woven(weave, k, mine, lag):
            if weave:
                m, b = weave
                if 2 <= k < 2 + TPB:
                    lag(m, b * TPB + k - 2)
                if k < TPB:
                    mine(m, b * TPB + k)

        def act_split(act, n, slot, width=PC):
            split_waits_raw(act, n, slot)
            if not isinstance(n, int) or n >= W_SLOTS:
                act.wait_ge(w_used, n - W_SLOTS + 1)
            nc.scalar.copy(w_hi[:, slot, 0:width], w_raw[:, slot, 0:width]).then_inc(hi_split, 1)

        def dve_split(dve, n, slot, width=PC):
            dve.wait_ge(hi_split, n + 1)
            nc.vector.tensor_tensor(w_lo[:, slot, 0:width], w_raw[:, slot, 0:width],
                                    w_hi[:, slot, 0:width].bitcast(F32), ALU.subtract).then_inc(lo_split, 1)

        def width_of(n):
            return BLOCKS[n // DT].width if n < PIECE_DOWN else PC

        steps = [(b, g, h, q) for b in range(NB) for g in "BA" for h in range(BH if g == "B" else AH)
                 for q in range(TPB)]
        PREP0 = [b * 2 * BH * TPB + 4 for b in range(NB)]
        PREP_EVERY = 5
        NPREP = AH // 2 + 1
        prep_at = {PREP0[b] + PREP_EVERY * j: ("q", b, j) for b in range(NB) for j in range(NPREP)}

        def attention_order(i):
            return (prep_at.get(i), i if i < NSTEP else None, i - LAG_T if 0 <= i - LAG_T < NSTEP else None,
                    i - LAG_V if 0 <= i - LAG_V < NSTEP else None)

        events = []
        for i in range(NSTEP + LAG_T):
            prep, _, t, _ = attention_order(i)
            events += [prep] if prep else []
            events += [("p", t)] if t is not None else []
        event_of = {e: k for k, e in enumerate(events)}

        def turn_bank(e):
            return ps[PT_BANKS[e % len(PT_BANKS)]]

        @block.tensor
        def _(pe):
            def three(out, a_hi, a_lo, b_hi, b_lo, first, last):
                nc.tensor.matmul(out, a_hi, b_hi, start=first, stop=False)
                nc.tensor.matmul(out, a_hi, b_lo, start=False, stop=False)
                return nc.tensor.matmul(out, a_lo, b_hi, start=False, stop=last)

            def products(slot, k, last_k, kind, lhs, banks, seqs, bank_wait, width=PC):
                lhs_hi, lhs_lo = lhs
                for pos, bank in enumerate(banks):
                    if k == 0:
                        bank_wait(pos, bank)
                    if kind == "tm":
                        t = seqs[0] * TPB + pos
                        mm = three(ps[bank][:, 0:width], lhs_hi[:, k, t * P:(t + 1) * P],
                                   lhs_lo[:, k, t * P:(t + 1) * P], w_hi[:, slot, 0:width], w_lo[:, slot, 0:width],
                                   k == 0, k == last_k)
                    else:
                        j, b = (pos // 2, pos % 2) if len(seqs) == 2 else (pos, seqs[0])
                        mm = three(ps[bank][:, :], w_hi[:, slot, j * P:(j + 1) * P], w_lo[:, slot, j * P:(j + 1) * P],
                                   lhs_hi[:, k, b * SEQ:(b + 1) * SEQ], lhs_lo[:, k, b * SEQ:(b + 1) * SEQ],
                                   k == 0, k == last_k)
                    if pos == len(banks) - 1:
                        mm.then_inc(w_used, 1)
                    elif k == last_k:
                        mm.then_inc(bank_full, 1)

            def run_block(i, bank_wait):
                blk = BLOCKS[i]
                kind = "fm" if blk.what in ("qb", "kb", "up") else "tm"
                for k in range(DT):
                    n = i * DT + k
                    pe.wait_ge(lo_split, n + 1)
                    products(n % W_SLOTS, k, DT - 1, kind, (hT_hi, hT_lo), blk.banks, blk.seqs, bank_wait, blk.width)
                    if blk.weave and 1 <= k < 1 + TPB:
                        pe_norm(pe, blk.weave[0], blk.weave[1] * TPB + k - 1)

            pe.wait_ge(const_landed, 16)
            for t in range(TPB):
                pe_norm(pe, 0, t)

            def wait_turned(m, t):
                pe.wait_ge(hT_hi_ready, 2 * (m * NT + t + 1))
                pe.wait_ge(hT_lo_ready, 2 * (m * NT + t + 1))

            def after_norm0(pos, bank):
                wait_turned(0, bank)
                if bank == TPB:
                    wait_turned(0, NT - 1)

            def after_tm(evacs):
                def wait(pos, bank):
                    pe.wait_ge(dve_evac if bank % 2 else act_evac, evacs + bank // 2 + 1)
                return wait

            def after_fm(evacs):
                def wait(pos, bank):
                    pe.wait_ge(dve_evac if bank >= 4 else act_evac, evacs + bank % 4 + 1)
                return wait

            run_block(0, after_norm0)
            run_block(1, after_norm0)
            run_block(2, after_tm(0))
            run_block(3, after_tm(4))
            run_block(4, after_tm(8))
            run_block(5, after_fm(12))

            def scores(i):
                b, g, h, q = steps[i]
                if i >= len(S_BANKS):
                    pe.wait_ge(p_ready, i - len(S_BANKS) + 1)
                out = ps[S_BANKS[i % len(S_BANKS)]]
                if g == "B":
                    t0 = b * SEQ
                    r = HD * (h % 2)
                    k0 = t0 + B_KEY_COL[q] * GH
                    mm = nc.tensor.matmul(out[:, 0:KW], qkb[r:r + HD, h // 2, t0 + q * P:t0 + (q + 1) * P],
                                          qkb[r:r + HD, BH * HD // P + h // 2, k0:k0 + KW], start=True, stop=True)
                else:
                    if h == 0 and q == 0:
                        pe.wait_ge(pt_copied, event_of[("q", b, NPREP - 1)] + 1)
                        pe.wait_ge(qk_lo_ready, (b + 1) * NPREP)
                    kv = h // 4
                    r = HD * kv
                    tok = slice(q * P, (q + 1) * P)
                    nc.tensor.matmul(out[:, :], q_hl[:, h, tok], k_hh[:, kv, :], start=True, stop=False)
                    mm = nc.tensor.matmul(out[:, :], q_hl[r:r + HD, h, tok], k_lo[r:r + HD, :], start=False, stop=True)
                mm.then_inc(s_ready, 1)

            def wait_turn_bank(e):
                back = e - len(PT_BANKS)
                if back >= 0:
                    pe.wait_ge(pt_copied, back + 1)
                    if events[back][0] == "q":
                        pe.wait_ge(qk_lo_ready, events[back][1] * NPREP + events[back][2] + 1)

            def transposes(i):
                b, g, h, q = steps[i]
                e = event_of[("p", i)]
                pe.wait_ge(p_ready, i + 1)
                wait_turn_bank(e)
                for k in range(KW // P if g == "B" else TPB):
                    last = nc.tensor.transpose(turn_bank(e)[:, k * P:(k + 1) * P],
                                               prob[:, i % PROB_SLOTS, k * P:(k + 1) * P], ident[:, :])
                last.then_inc(pt_ready, 1)

            def turn_qk(ev):
                _, b, j = ev
                e = event_of[ev]
                if j == 0:
                    pe.wait_ge(rope_done, (b + 1) * TPB)
                wait_turn_bank(e)
                c0 = TKA if j == 0 else (j - 1) * P
                for q in range(TPB):
                    last = nc.tensor.transpose(turn_bank(e)[:, q * P:(q + 1) * P],
                                               pj[:, b * TPB + q, c0:c0 + P], ident[:, :])
                last.then_inc(pt_ready, 1)

            def values(i):
                b, g, h, q = steps[i]
                pe.wait_ge(pt_copied, event_of[("p", i)] + 1)
                head = i // TPB
                if q == 0 and head >= len(O_BANKS):
                    pe.wait_ge(oT_ready, head - len(O_BANKS) + 1)
                if i == 1:
                    pe.wait_ge(vsh_landed, 16 * 2 * NB)
                nk = KW // P if g == "B" else TPB
                for k in range(nk):
                    if g == "A":
                        v = pj[:, b * TPB + k, TVA + HD * (h // 4):TVA + HD * (h // 4) + HD]
                    elif q in (0, TPB - 1):
                        v = pj[:, b * TPB + (0 if q == 0 else TPB - 2) + k, TVB + HD * h:TVB + HD * (h + 1)]
                    else:
                        v = vsh[:, b, q - 1 + k, HD * h:HD * (h + 1)]
                    mm = nc.tensor.matmul(ps[O_BANKS[head % len(O_BANKS)]][0:HD, q * P:(q + 1) * P], v,
                                          probT[:, i % PT_SLOTS, k * P:(k + 1) * P],
                                          start=(k == 0), stop=(k == nk - 1))
                mm.then_inc(pv_done, 1)

            def turn_back(head):
                pe.wait_ge(oT_ready, head + 1)
                if head:
                    pe.wait_ge(y_written, head)
                for q in range(TPB):
                    last = nc.tensor.transpose(ps[BACK_BANK][:, q * HD:(q + 1) * HD],
                                               oT[:, head % 2, q * P:(q + 1) * P], ident[0:HD, 0:HD])
                last.then_inc(back_ready, 1)

            pe.wait_ge(act_evac, ACT0)
            pe.wait_ge(dve_evac, DVE0)
            for i in range(NSTEP + LAG_BACK):
                prep, s, t, v = attention_order(i)
                if prep:
                    turn_qk(prep)
                if s is not None:
                    scores(s)
                if t is not None:
                    transposes(t)
                if v is not None:
                    values(v)
                j = i - LAG_BACK + 1
                if j >= 0 and j % TPB == TPB - 1:
                    turn_back(j // TPB)

            for t in range(TPB):
                pe_norm(pe, 1, t)

            def out_wait(i):
                def wait(pos, bank):
                    if i in (0, 2):
                        wait_turned(1, (i // 2) * TPB + pos)
                    if i == 0 and pos == 0:
                        wait_turned(1, TPB - 1)
                        pe.wait_ge(y_written, NSTEP // TPB)
                    g = 4 * i + pos
                    if g >= OUT_BANKS:
                        pe.wait_ge(dve_evac, DVE0 + g - OUT_BANKS + 1)
                return wait

            for i in range(N_OUT):
                run_block(N_PJ + i, out_wait(i))

            def up0_wait(pos, bank):
                pe.wait_ge(dve_evac, DVE1 - 4 + min(bank, 3) + 1)
                if bank == 0:
                    wait_turned(2, TPB - 1)
                if bank == 4:
                    wait_turned(2, NT - 1)

            run_block(N_PJ + N_OUT, up0_wait)
            run_block(N_PJ + N_OUT + 1, up0_wait)

            def down(c, first, u_before):
                a0 = c * UP_ACT + ACT0
                d0 = c * CH_DVE + DVE1

                def after_relu(pos, bank):
                    if bank < 4:
                        pe.wait_ge(act_evac, a0 + (bank + 1))
                    else:
                        pe.wait_ge(dve_evac, d0 + (bank - 4 + 1))

                def after_add(pos, bank):
                    pe.wait_ge(dve_evac, d0 + (UP_DVE + bank + 1))

                for half in range(2):
                    for k in range(FT):
                        n = half * FT + k
                        pe.wait_ge(lo_split, first + (n + 1))
                        if half == 0:
                            pe.wait_ge(u_hi_ready, u_before(k))
                            pe.wait_ge(u_lo_ready, u_before(k))
                        products(n % W_SLOTS, k, FT - 1, "tm", (u_hi, u_lo), list(range(NT)), (0,),
                                 after_add if half else after_relu)

            down(0, PIECE_DOWN, lambda k: 4 + k + 1)
            with pe.Fori(1, NCHUNK) as c:
                base = c * PER_CHUNK + (PIECE_LOOP - PER_CHUNK)
                d0 = c * CH_DVE + DVE1

                def up_wait(pos, bank):
                    pe.wait_ge(dve_evac, d0 - NT + bank + 1)

                for k in range(DT):
                    pe.wait_ge(lo_split, base + (k + 1))
                    products(k % W_SLOTS, k, DT - 1, "fm", (hT_hi, hT_lo), FM_BANKS, (0, 1), up_wait)
                down(c, base + DT, lambda k: c * 8 + (2 * k + 2))

        @block.scalar
        def _(act):
            square = lambda m, t: act_square(act, m, t)
            hT_hi_of = lambda m, t: act_hT_hi(act, m, t)

            def take(i):
                blk = BLOCKS[i]
                for pos, bank in enumerate(blk.banks):
                    if blk.what in ("qb", "kb"):
                        j, b = pos // 2, pos % 2
                        mine, part = b == 0, (4 if blk.what == "kb" else 0) + j
                    else:
                        mine = bank % 2 == 0
                    if not mine:
                        continue
                    wait_bank(act, FULL_BEFORE[i], pos, len(blk.banks), DT * (i + 1) - 1)
                    if blk.what in ("qb", "kb"):
                        ins = nc.scalar.mul(qkb[:, part, 0:SEQ], ps[bank][:, :], QSCALE if blk.what == "qb" else 1.0)
                    else:
                        c0 = {"qa": TQA, "kv": TKA, "vb": TVB}[blk.what]
                        ins = nc.scalar.copy(pj[:, bank, c0:c0 + blk.width], ps[bank][:, 0:blk.width])
                    ins.then_inc(act_evac, 1)

            def hidden_relu(c, s, bank):
                if s >= 2:
                    act.wait_ge(sq_ready, c * 8 + (s - 1))
                nc.scalar.activation(relu[:, s % 2, :], ps[bank][:, :], ACT.Relu).then_inc(act_evac, 1)

            def hidden_hi(c, s, j, b):
                act.wait_ge(sq_ready, c * 8 + (s + 1))
                nc.scalar.copy(u_hi[:, j, b * SEQ:(b + 1) * SEQ], sq[:, s % 2, :]).then_inc(u_hi_ready, 1)

            def run_blocks(i0, i1, at_end):
                for i in range(i0, i1):
                    for k in range(DT):
                        n = i * DT + k + W_SLOTS
                        if k == DT - 1:
                            at_end(i)
                        woven(BLOCKS[i].weave, k, square, hT_hi_of)
                        act_split(act, n, n % W_SLOTS, width_of(n))
                        if n == HSUM_AT + NT:
                            act.wait_ge(hstat, 2 * NT)
                            nc.scalar.activation(hss[:, :, :], hss[:, :, :], ACT.Sqrt, bias=eps[:, 0:1],
                                                 scale=1.0 / HD).then_inc(hrms_ready, 1)

            act.wait_ge(eps_ready, 1)
            norm_alone(0, 0, square, hT_hi_of, lambda n: act_split(act, n, n % W_SLOTS, width_of(n)))

            def pj_end(i):
                if BLOCKS[i].what == "qb":
                    act.wait_ge(bias_ready, 1)
                take(i)

            run_blocks(0, N_PJ, pj_end)

            def softmax_exp(i):
                b, g, h, q = steps[i]
                act.wait_ge(max_ready, i + 1)
                if i >= PROB_SLOTS:
                    act.wait_ge(pt_ready, event_of[("p", i - PROB_SLOTS)] + 1)
                src, n = (sB[:, i % PROB_SLOTS, :], KW) if g == "B" else (ps[S_BANKS[i % len(S_BANKS)]][:, :], SEQ)
                nc.scalar.activation(prob[:, i % PROB_SLOTS, 0:n], src, ACT.Exp, bias=negmax[:, i:i + 1],
                                     accum_out=psums[:, i:i + 1]).then_inc(p_ready, 1)

            def copy_turned(ev):
                e = event_of[ev]
                bank = turn_bank(e)
                act.wait_ge(pt_ready, e + 1)
                top, bottom = slice(0, HD), slice(HD, P)
                if ev[0] == "q" and ev[2] == 0:
                    for kv, rows in enumerate((top, bottom)):
                        for dst in (rows, bottom if kv == 0 else top):
                            ins = nc.scalar.copy(k_hh[dst, kv, :], bank[rows, :])
                elif ev[0] == "q":
                    h = ev[2] - 1
                    nc.scalar.mul(q_hl[top, h, :], bank[top, :], QSCALE)
                    ins = nc.scalar.mul(q_hl[bottom, h + 4, :], bank[bottom, :], QSCALE)
                else:
                    i = ev[1]
                    if i >= PT_SLOTS:
                        act.wait_ge(pv_done, i - PT_SLOTS + 1)
                    n = KW if steps[i][1] == "B" else SEQ
                    ins = nc.scalar.copy(probT[:, i % PT_SLOTS, 0:n], bank[:, 0:n])
                ins.then_inc(pt_copied, 1)

            for i in range(NSTEP + LAG_T):
                prep, s, t, _ = attention_order(i)
                if prep:
                    copy_turned(prep)
                if t is not None:
                    copy_turned(("p", t))
                if s is not None:
                    softmax_exp(s)

            norm_alone(1, 0, square, hT_hi_of)
            run_blocks(N_PJ, N_PJ + N_OUT, lambda i: None)

            def up0_end(i):
                b = i - (N_PJ + N_OUT)
                for j in range(FT):
                    s = b * FT + j
                    if b == 0:
                        wait_bank(act, FULL_BEFORE[i], j, FT, DT * (i + 1) - 1)
                        hidden_relu(0, s, j)
                    if s >= 1:
                        hidden_hi(0, s - 1, (s - 1) % FT, (s - 1) // FT)
                if b == 1:
                    hidden_hi(0, 2 * FT - 1, FT - 1, 1)

            run_blocks(N_PJ + N_OUT, N_PJ + N_OUT + 2, up0_end)
            for n in range(PIECE_DOWN + W_SLOTS, PIECE_LOOP + W_SLOTS):
                act_split(act, n, n % W_SLOTS)

            def mlp_chunk(c, last):
                first = c * PER_CHUNK + (PIECE_LOOP - PER_CHUNK)

                def split(k0, k1):
                    for k in range(k0, k1):
                        if not (last and k >= PER_CHUNK):
                            act_split(act, first + k, k % W_SLOTS)

                split(W_SLOTS, DT + W_SLOTS - 1)
                for s in range(8):
                    if s % 2 == 0:
                        wait_bank(act, c * FULL_CHUNK + (FULL_LOOP - FULL_CHUNK), s, NT, None)
                        hidden_relu(c, s, s // 2)
                    if s >= 1:
                        hidden_hi(c, s - 1, (s - 1) // 2, (s - 1) % 2)
                hidden_hi(c, 7, 3, 1)
                split(DT + W_SLOTS - 1, PER_CHUNK + W_SLOTS)

            with act.Fori(1, NCHUNK - 1) as c:
                mlp_chunk(c, False)
            mlp_chunk(NCHUNK - 1, True)

            END = DVE1 + NCHUNK * CH_DVE
            for t in range(NT):
                act.wait_ge(dve_evac, END - 2 * NT + t + 1)
                if t == 0:
                    act.wait_ge(w_used, PIECE_LOOP + (NCHUNK - 1) * PER_CHUNK - 2 * FT)
                nc.scalar.activation(junk[:, t, 0:PC], xr[:, t, 0:PC], ACT.Square,
                                     accum_out=stat[:, 3, t, 0:1]).then_inc(sumsq, 1)
            act.wait_ge(half_ready, 1)
            for t in range(NT):
                act.wait_ge(dve_evac, END - NT + t + 1)
                nc.scalar.activation(junk[:, t, PC:D], xr[:, t, PC:D], ACT.Square,
                                     accum_out=stat[:, 3, t, 1:2]).then_inc(sumsq, 1)
                act.wait_ge(sumsq, SQ0[3] + NT + t + 1)
                nc.scalar.activation(rms[:, 3, t, 0:1], stat[:, 3, t, 1:2], ACT.Sqrt, bias=half_ms[:, t:t + 1],
                                     scale=1.0 / D).then_inc(rms_ready, 1)

        @block.vector
        def _(dve):
            norm = lambda m, t: dve_norm(dve, m, t)
            hT_lo_of = lambda m, t: dve_hT_lo(dve, m, t)

            def take(i):
                blk = BLOCKS[i]
                for pos, bank in enumerate(blk.banks):
                    if blk.what in ("qb", "kb"):
                        j, b = pos // 2, pos % 2
                        mine, part = b == 1, (4 if blk.what == "kb" else 0) + j
                    else:
                        mine = bank % 2 == 1
                    if not mine:
                        continue
                    wait_bank(dve, FULL_BEFORE[i], pos, len(blk.banks), DT * (i + 1) - 1)
                    if blk.what in ("qb", "kb"):
                        ins = nc.vector.tensor_scalar(qkb[:, part, SEQ:TOK], ps[bank][:, :],
                                                      QSCALE if blk.what == "qb" else 1.0, None, ALU.mult)
                    else:
                        c0 = {"qa": TQA, "kv": TKA, "vb": TVB}[blk.what]
                        ins = nc.vector.tensor_copy(pj[:, bank, c0:c0 + blk.width], ps[bank][:, 0:blk.width])
                    ins.then_inc(dve_evac, 1)

            def add_residual(full_before, pos, nbanks, last_piece, bank, t, half):
                wait_bank(dve, full_before, pos, nbanks, last_piece)
                nc.vector.tensor_tensor(xr[:, t, half * PC:(half + 1) * PC], ps[bank][:, :],
                                        xr[:, t, half * PC:(half + 1) * PC], ALU.add).then_inc(dve_evac, 1)

            def hidden_relu(c, s, bank, dve_done):
                if s >= 2:
                    dve.wait_ge(sq_ready, c * 8 + (s - 1))
                nc.vector.tensor_scalar(relu[:, s % 2, :], ps[bank][:, :], 0.0, None, ALU.max).then_inc(dve_evac, 1)
                dve.wait_ge(dve_evac, c * CH_DVE + (DVE1 + dve_done))

            def hidden_square(c, s):
                if s >= 2:
                    dve.wait_ge(u_lo_ready, c * 8 + (s - 1))
                nc.vector.tensor_tensor(sq[:, s % 2, :], relu[:, s % 2, :], relu[:, s % 2, :],
                                        ALU.mult).then_inc(sq_ready, 1)

            def hidden_lo(c, s, j, b):
                dve.wait_ge(u_hi_ready, c * 8 + (s + 1))
                tok = slice(b * SEQ, (b + 1) * SEQ)
                nc.vector.tensor_tensor(u_lo[:, j, tok], sq[:, s % 2, :], u_hi[:, j, tok].bitcast(F32),
                                        ALU.subtract).then_inc(u_lo_ready, 1)

            def head_sums(t):
                dve.wait_ge(act_evac, 8)
                dve.wait_ge(dve_evac, 8)
                if t >= 1:
                    dve.wait_ge(hstat, 2 * t)
                qk = pj[:, t, 0:QKW]
                nc.vector.tensor_tensor(rt[:, 0, :], qk, qk, ALU.mult).then_inc(hstat, 1)
                dve.wait_ge(hstat, 2 * t + 1)
                nc.vector.tensor_reduce(hss[:, t, :], rt[:, 0, :].rearrange("p (h d) -> p h d", d=HD), AX_X,
                                        ALU.add).then_inc(hstat, 1)

            def head_reciprocals():
                dve.wait_ge(hrms_ready, 1)
                nc.vector.reciprocal(hss[:, :, :], hss[:, :, :]).then_inc(hstat_ready, 1)

            def run_blocks(i0, i1, at_end):
                for i in range(i0, i1):
                    for k in range(DT):
                        n = i * DT + k + W_SLOTS
                        if k == DT - 1:
                            at_end(i)
                        woven(BLOCKS[i].weave, k, norm, hT_lo_of)
                        dve_split(dve, n, n % W_SLOTS, width_of(n))
                        if HSUM_AT <= n < HSUM_AT + NT:
                            head_sums(n - HSUM_AT)
                        if n == HSUM_AT + NT + 1:
                            head_reciprocals()

            norm_alone(0, 0, norm, hT_lo_of, lambda n: dve_split(dve, n, n % W_SLOTS, width_of(n)))

            def pj_end(i):
                if BLOCKS[i].what == "qb":
                    dve.wait_ge(bias_ready, 1)
                take(i)

            run_blocks(0, N_PJ, pj_end)

            def row_max(i):
                b, g, h, q = steps[i]
                dve.wait_ge(s_ready, i + 1)
                if g == "B":
                    if i >= PROB_SLOTS:
                        dve.wait_ge(p_ready, i - PROB_SLOTS + 1)
                    nb = b * BH * TPB + h * TPB + q
                    nc.vector.tensor_tensor(sB[:, i % PROB_SLOTS, :], ps[S_BANKS[i % len(S_BANKS)]][:, 0:KW],
                                            biasm[:, B_VARIANT[q], h, :], ALU.add).then_inc(biased, 1)
                    dve.wait_ge(biased, nb + 1)
                    src = sB[:, i % PROB_SLOTS, :]
                else:
                    src = ps[S_BANKS[i % len(S_BANKS)]][:, :]
                nc.vector.reduce_max(negmax[:, i:i + 1], src, AX_X, negate=True).then_inc(max_ready, 1)

            def take_head(head):
                dve.wait_ge(pv_done, (head + 1) * TPB)
                if head >= 2:
                    dve.wait_ge(back_ready, head - 1)
                nc.vector.tensor_copy(oT[:, head % 2, :],
                                      ps[O_BANKS[head % len(O_BANKS)]][0:HD, :]).then_inc(oT_ready, 1)

            def head_out(head):
                b, g, h, _ = steps[head * TPB]
                dve.wait_ge(p_ready, (head + 1) * TPB)
                nc.vector.reciprocal(pinv[:, head * TPB:(head + 1) * TPB],
                                     psums[:, head * TPB:(head + 1) * TPB]).then_inc(inv_ready, 1)
                dve.wait_ge(inv_ready, head + 1)
                dve.wait_ge(back_ready, head + 1)
                if head == 0:
                    dve.wait_ge(vsh_landed, 16 * 2 * NB)
                c0 = (TQA if g == "A" else TVB) + h * HD
                nc.vector.tensor_tensor(pj[:, b * TPB:(b + 1) * TPB, c0:c0 + HD],
                                        ps[BACK_BANK][:, 0:TPB * HD].rearrange("p (q d) -> p q d", d=HD),
                                        over(pinv[:, head * TPB:(head + 1) * TPB], 2, HD),
                                        ALU.mult).then_inc(y_written, 1)

            def qk_low(ev):
                _, b, j = ev
                e = event_of[ev]
                bank = turn_bank(e)
                dve.wait_ge(pt_copied, e + 1)
                top, bottom = slice(0, HD), slice(HD, P)
                if j == 0:
                    for kv, rows in enumerate((top, bottom)):
                        ins = nc.vector.tensor_tensor(k_lo[rows, :], bank[rows, :], k_hh[rows, kv, :].bitcast(F32),
                                                      ALU.subtract)
                else:
                    for h, rows, other in ((j - 1, top, bottom), (j + 3, bottom, top)):
                        ins = nc.vector.scalar_tensor_tensor(q_hl[other, h, :], bank[rows, :], QSCALE,
                                                             q_hl[rows, h, :].bitcast(F32), ALU.mult, ALU.subtract)
                ins.then_inc(qk_lo_ready, 1)

            for i in range(NSTEP + LAG_BACK + 1):
                prep = prep_at.get(i)
                if prep:
                    qk_low(prep)
                if i < NSTEP:
                    row_max(i)
                j = i - LAG_V - 1
                if 0 <= j < NSTEP and j % TPB == TPB - 1:
                    take_head(j // TPB)
                j = i - LAG_BACK
                if j >= 0 and j % TPB == TPB - 1:
                    head_out(j // TPB)

            norm_alone(1, 0, norm, hT_lo_of)
            dve.wait_ge(xr_landed, 16 * NT)

            def out_end(i):
                o = i - N_PJ
                for pos, bank in enumerate(BLOCKS[i].banks):
                    add_residual(FULL_BEFORE[i], pos, 4, DT * (i + 1) - 1, bank, (o // 2) * TPB + pos, o % 2)

            run_blocks(N_PJ, N_PJ + N_OUT, out_end)

            def up0_end(i):
                b = i - (N_PJ + N_OUT)
                for j in range(FT):
                    s = b * FT + j
                    if b == 0:
                        dve.wait_ge(act_evac, ACT0 + j + 1)
                    else:
                        wait_bank(dve, FULL_BEFORE[i], j, FT, DT * (i + 1) - 1)
                        hidden_relu(0, s, FT + j, j + 1)
                    hidden_square(0, s)
                    if s >= 1:
                        hidden_lo(0, s - 1, (s - 1) % FT, (s - 1) // FT)
                if b == 1:
                    hidden_lo(0, 2 * FT - 1, FT - 1, 1)
                    dve.wait_ge(u_lo_ready, 8)

            run_blocks(N_PJ + N_OUT, N_PJ + N_OUT + 2, up0_end)

            def down(c, full, first, split):
                split(W_SLOTS - 1, FT + W_SLOTS - 1)
                for t in range(NT):
                    add_residual(full, t, NT, first + (FT - 1), t, t, 0)
                split(FT + W_SLOTS - 1, 2 * FT + W_SLOTS - 1)
                for t in range(NT):
                    add_residual(full + (NT - 1), t, NT, first + (2 * FT - 1), t, t, 1)
                split(2 * FT + W_SLOTS - 1, 2 * FT + W_SLOTS)

            def split0(k0, k1):
                for k in range(max(k0, W_SLOTS), k1):
                    dve_split(dve, PIECE_DOWN + k, k % W_SLOTS)

            down(0, FULL_DOWN, PIECE_DOWN, split0)

            def mlp_chunk(c, last):
                first = c * PER_CHUNK + (PIECE_LOOP - PER_CHUNK)
                full = c * FULL_CHUNK + (FULL_LOOP - FULL_CHUNK)

                def split(k0, k1):
                    for k in range(k0, k1):
                        if not (last and k >= PER_CHUNK):
                            dve_split(dve, first + k, k % W_SLOTS)

                split(W_SLOTS, DT + W_SLOTS - 1)
                for s in range(8):
                    if s % 2 == 0:
                        dve.wait_ge(act_evac, c * UP_ACT + (ACT0 + s // 2 + 1))
                    else:
                        wait_bank(dve, full, s, NT, first + (DT - 1))
                        hidden_relu(c, s, 4 + s // 2, s // 2 + 1)
                    hidden_square(c, s)
                    if s >= 1:
                        hidden_lo(c, s - 1, (s - 1) // 2, (s - 1) % 2)
                hidden_lo(c, 7, 3, 1)
                dve.wait_ge(u_lo_ready, c * 8 + 8)
                if not last:
                    down(c, full + (NT - 1), first + DT, lambda k0, k1: split(DT + k0, DT + k1))
                    return
                full = full + (NT - 1)
                split(DT + W_SLOTS - 1, DT + FT + W_SLOTS - 1)
                for t in range(NT):
                    add_residual(full, t, NT, first + (DT + FT - 1), t, t, 0)
                dve.wait_ge(sumsq, SQ0[3] + NT)
                nc.vector.tensor_scalar(half_ms[:, :], stat[:, 3, :, 0], 1.0 / D, EPS, ALU.mult,
                                        ALU.add).then_inc(half_ready, 1)
                split(DT + FT + W_SLOTS - 1, PER_CHUNK)
                for t in range(NT + 1):
                    if t < NT:
                        add_residual(full + (NT - 1), t, NT, first + (PER_CHUNK - 1), t, t, 1)
                    if t:
                        dve.wait_ge(rms_ready, 3 * NT + t)
                        nc.vector.reciprocal(rstd[:, 3, t - 1, 0:1], rms[:, 3, t - 1, 0:1]).then_inc(rstd_ready, 1)
                        dve.wait_ge(rstd_ready, 3 * NT + t)
                        dve.wait_ge(xg_ready, NT + t)
                        nc.vector.tensor_scalar(yo[:, t - 1, :], yo[:, t - 1, :], rstd[:, 3, t - 1, 0:1], None,
                                                ALU.mult).then_inc(xo_ready, 1)

            with dve.Fori(1, NCHUNK - 1) as c:
                mlp_chunk(c, False)
            mlp_chunk(NCHUNK - 1, True)

        @block.gpsimd
        def _(pool):
            count = [0]

            def step(ins):
                count[0] += 1
                ins.then_inc(pool_step, 1)
                pool.wait_ge(pool_step, count[0])

            nc.gpsimd.memset(eps[:, :], EPS).then_inc(eps_ready, 1)
            step(nc.gpsimd.memset(biasm[:, :, :, :], MASKED))
            pool.wait_ge(pool_landed, 16 * (3 + BH))
            for v, (w0, z0, n) in enumerate(B_VALID):
                for h in range(BH):
                    fwd = bias_raw[:, h, ::-1].rearrange("p (k z) -> p z k", z=NZ)
                    last = nc.gpsimd.tensor_tensor(
                        biasm[:, v, h, w0 * GH:(w0 + n) * GH].rearrange("p (z k) -> p z k", k=GH),
                        fwd[:, z0:z0 + n, :],
                        mask[:, v, z0 * GH:(z0 + n) * GH].rearrange("p (z k) -> p z k", k=GH), ALU.add)
            last.then_inc(bias_ready, 1)
            for a in range(4):
                last = nc.gpsimd.tensor_tensor(tab[:, a, :, :], rope[:, a % 2, :, :], over(qkg[:, a, :], 1, TPB),
                                               ALU.mult)
            step(last)

            pool.wait_ge(xT_ready, 2 * NT)
            for t in range(NT):
                q = t % TPB
                if t == 0:
                    pool.wait_ge(hstat_ready, 1)
                qk = pj[:, t, 0:QKW]
                heads = qk.rearrange("p (h d) -> p h d", d=HD)
                step(nc.gpsimd.tensor_tensor(heads, heads, over(hss[:, t, :], 2, HD), ALU.mult))
                for a, h0, h1 in ((0, 0, AH), (2, AH, AH + KVH)):
                    own = heads[:, h0:h1, :]
                    nh = h1 - h0
                    c = rt[:, 1, h0 * HD:h1 * HD].rearrange("p (h d) -> p h d", d=HD)
                    last = nc.gpsimd.tensor_tensor(c, own, over(tab[:, a, q, :], 1, nh), ALU.mult)
                    halves = own.rearrange("p h (x y e) -> p h x y e", x=2, y=2)
                    out = rt[:, 2, h0 * HD:h1 * HD].rearrange("p (h x y e) -> p h x y e", h=nh, x=2, y=2)
                    sin = tab[:, a + 1, q, :].rearrange("p (x y e) -> p x y e", x=2, y=2)
                    for y in range(2):
                        last = nc.gpsimd.tensor_tensor(out[:, :, :, y, :], halves[:, :, :, 1 - y, :],
                                                       over(sin[:, :, y, :], 1, nh), ALU.mult)
                step(last)
                nc.gpsimd.tensor_tensor(pj[:, t, TKA:TVA], rt[:, 1, TKA:TVA], rt[:, 2, TKA:TVA], ALU.add)
                pair = "p (g h d) -> p g h d"
                nc.gpsimd.tensor_tensor(pj[:, t, 0:TKA].rearrange("p (h g d) -> p g h d", g=2, d=HD),
                                        rt[:, 1, 0:TKA].rearrange(pair, g=2, d=HD),
                                        rt[:, 2, 0:TKA].rearrange(pair, g=2, d=HD), ALU.add).then_inc(rope_done, 1)

            pool.wait_ge(gain_landed, 16 * 4)
            pool.wait_ge(w_used, PIECE_LOOP + (NCHUNK - 1) * PER_CHUNK - 2 * FT)
            for half in range(2):
                for t in range(NT):
                    pool.wait_ge(dve_evac, DVE1 + NCHUNK * CH_DVE - (2 - half) * NT + t + 1)
                    cols = slice(half * PC, (half + 1) * PC)
                    nc.gpsimd.tensor_tensor(yo[:, t, cols], xr[:, t, cols], gain[:, cols], ALU.mult).then_inc(xg_ready, 1)


def kernel(**inputs):
    import concourse.bacc as bacc
    from concourse.bass_utils import run_bass_kernel_spmd

    nc = bacc.Bacc("TRN2", target_bir_lowering=False, num_devices=1)
    arrays = {}

    def dram(name, a):
        a = np.ascontiguousarray(a)
        arrays[name] = a
        return nc.dram_tensor(name, a.shape, mybir.dt.from_np(a.dtype), kind="ExternalInput").ap()

    x = [dram(n, np.asarray(inputs[n]).reshape(SEQ, D)) for n in ("x_prompt", "x_sample")]
    w = {n: dram(n, np.asarray(inputs[n])[0]) for n in ("w_in", "w_out", "w_up", "w_down")}
    bias = np.asarray(inputs["nat_rel_bias"])[0, :, ::-1, ::-1].reshape(BH, -1)
    bias = np.pad(bias, ((0, 0), (BPAD, BLEN - BPAD - bias.shape[1])))
    out_norm = np.concatenate([np.asarray(inputs["out_norm_a_g"])[0], np.asarray(inputs["out_norm_b_g"])[0]])
    gains = np.stack([np.asarray(inputs["norm_attn_g"])[0], out_norm, np.asarray(inputs["norm_mlp_g"])[0],
                      np.asarray(inputs["final_norm_g"])])

    def swapped(g):
        return g.reshape(2, 2, HD // 4)[:, ::-1].reshape(HD)

    qg, kg = np.asarray(inputs["q_norm_g"])[0], np.asarray(inputs["k_norm_g"])[0]
    rope_c, mask_c, ident_c = shape_constants()
    ys = [nc.dram_tensor(n, (SEQ, D), F32, kind="ExternalOutput").ap() for n in ("y_prompt", "y_sample")]
    qk_gains = np.concatenate([qg, swapped(qg), kg, swapped(kg)])[None]
    encoder_program(nc, x, w["w_in"], dram("bias_tab", bias), dram("gains", gains), dram("qk_gains", qk_gains),
                    w["w_out"], w["w_up"], w["w_down"], dram("rope_c", rope_c), dram("mask_c", mask_c),
                    dram("ident_c", ident_c), ys)
    r = run_bass_kernel_spmd(nc, [arrays], core_ids=[0])
    return tuple(r.results[0][n].reshape(1, SEQ, D) for n in ("y_prompt", "y_sample"))
```
